# Optimizing a Trainium2 kernel written in Bass

```python
import math
import jax, jax.numpy as jnp
from jax import lax
import numpy as np

D_MODEL = 1024
BATCH = 1
SEQ = 128
DEPTH = 1
DEC_BATCH = 1
DEC_SEQ = 512
PAST_LEN = 128

GRID_W = 64
EPS = 1e-6
HY_CH = 512
HY_SHORT = 3
HY_EMB = 33
HY_FILT_HID = 64
HY_MIN_DECAY = math.log(1e-2) / 1.5
HY_MAX_DECAY = math.log(1e-2) / 0.3
GLA_HEADS = 4
GLA_DK = 64
GLA_DV = 128
GLA_KEY = GLA_HEADS * GLA_DK
GLA_VAL = GLA_HEADS * GLA_DV
GLA_RANK = 16
GLA_GATE_NORM = 16.0
GLA_CHUNK = 64
MIX_W = HY_CH + GLA_VAL
IN_COLS = 3 * HY_CH + 2 * GLA_KEY + 2 * GLA_VAL + 2 * GLA_RANK
PEER_HEADS = 8
PEER_NKEYS = 128
PEER_EXPERTS = PEER_NKEYS * PEER_NKEYS
PEER_DQ = 256
PEER_TOPK = 16
PEER_BLOCK = 128

kernel_name = "hyena_gla_peer_diffusion_step"

def rms_norm(x, g):
    xf = x.astype(jnp.float32)
    y = xf * lax.rsqrt(jnp.mean(xf * xf, axis=-1, keepdims=True) + EPS)
    return (y * g.astype(jnp.float32)).astype(x.dtype)

def short_conv(u, w, b, row_len):
    B, L, C = u.shape
    ur = u.reshape(B, L // row_len, row_len, C)
    pad = HY_SHORT // 2
    up = jnp.pad(ur, ((0, 0), (0, 0), (pad, pad), (0, 0)))
    y = sum(up[:, :, j:j + row_len] * w[j] for j in range(HY_SHORT)) + b
    return y.reshape(B, L, C)

def hyena_filter(L, w1, b1, w2, b2, w3, freq):
    f32 = jnp.float32
    t = jnp.linspace(0.0, 1.0, L, dtype=f32)[:, None]
    bands = (HY_EMB - 1) // 2
    w = 2.0 * math.pi * jnp.arange(L, dtype=f32)[:, None] / L
    f = jnp.linspace(1e-4, bands - 1, bands, dtype=f32)[None, :]
    z = jnp.concatenate([t, jnp.cos(f * w), -jnp.sin(f * w)], axis=-1)
    fr = freq.astype(f32)
    h = jnp.sin(fr * (z @ w1.astype(f32) + b1.astype(f32)))
    h = jnp.sin(fr * (h @ w2.astype(f32) + b2.astype(f32)))
    h = h @ w3.astype(f32)
    deltas = jnp.abs(jnp.linspace(HY_MIN_DECAY, HY_MAX_DECAY, HY_CH, dtype=f32))
    decay = jnp.exp(-t * deltas[None, :])
    return h[:, :HY_CH] * decay, h[:, HY_CH:] * decay

def hyena_mix(u, row_len, conv_w, conv_b, w1, b1, w2, b2, w3, freq, bias):
    B, L, _ = u.shape
    uc = short_conv(u, conv_w, conv_b, row_len).astype(jnp.float32)
    x0, x1, v = jnp.split(uc, 3, axis=-1)
    z = v * x1
    h_f, h_b = hyena_filter(L, w1, b1, w2, b2, w3, freq)
    k_full = jnp.concatenate([h_f, jnp.zeros((1, HY_CH), jnp.float32), h_b[1:][::-1]], axis=0)
    zf = jnp.fft.rfft(z, n=2 * L, axis=1)
    kf = jnp.fft.rfft(k_full, axis=0)
    y = jnp.fft.irfft(zf * kf[None], n=2 * L, axis=1)[:, :L]
    y = y + z * bias.astype(jnp.float32)
    return (y * x0).astype(u.dtype)

def gla_scan(q, k, v, log_a, s0):
    B, L, H, DK = q.shape
    DV = v.shape[-1]
    n = L // GLA_CHUNK

    def to_chunks(a):
        return a.reshape(B, n, GLA_CHUNK, H, a.shape[-1]).transpose(1, 0, 3, 2, 4)

    tri = jnp.tril(jnp.ones((GLA_CHUNK, GLA_CHUNK), dtype=bool))

    def step(S, inp):
        qc, kc, vc, ac = inp
        b = jnp.cumsum(ac, axis=2)
        inter = jnp.einsum('bhtd,bhde->bhte', qc * jnp.exp(b), S)
        diff = b[:, :, :, None, :] - b[:, :, None, :, :]
        dec = jnp.exp(jnp.where(tri[:, :, None], diff, -jnp.inf))
        att = jnp.einsum('bhtd,bhsd,bhtsd->bhts', qc, kc, dec)
        intra = jnp.einsum('bhts,bhse->bhte', att, vc)
        b_end = b[:, :, -1:, :]
        S_new = jnp.exp(b_end[:, :, 0, :])[..., None] * S + jnp.einsum(
            'bhsd,bhse->bhde', kc * jnp.exp(b_end - b), vc)
        return S_new, inter + intra

    S, o = lax.scan(step, s0, (to_chunks(q), to_chunks(k), to_chunks(v), to_chunks(log_a)))
    return o.transpose(1, 0, 3, 2, 4).reshape(B, L, H, DV), S

def gla_mix(q, k, v, og, lr, s0_f, s0_b, w2_f, b_f, w2_b, b_b, gnorm):
    f32 = jnp.float32
    B, L, _ = q.shape
    qh = q.astype(f32).reshape(B, L, GLA_HEADS, GLA_DK) * (GLA_DK ** -0.5)
    kh = k.astype(f32).reshape(B, L, GLA_HEADS, GLA_DK)
    vh = v.astype(f32).reshape(B, L, GLA_HEADS, GLA_DV)
    lrf = lr.astype(f32)
    la_f = (jax.nn.log_sigmoid(lrf[..., :GLA_RANK] @ w2_f.astype(f32) + b_f.astype(f32))
            / GLA_GATE_NORM).reshape(B, L, GLA_HEADS, GLA_DK)
    la_b = (jax.nn.log_sigmoid(lrf[..., GLA_RANK:] @ w2_b.astype(f32) + b_b.astype(f32))
            / GLA_GATE_NORM).reshape(B, L, GLA_HEADS, GLA_DK)
    o_f, s_f = gla_scan(qh, kh, vh, la_f, s0_f)
    o_b, s_b = gla_scan(qh[:, ::-1], kh[:, ::-1], vh[:, ::-1], la_b[:, ::-1], s0_b)
    o = rms_norm(o_f + o_b[:, ::-1], gnorm)
    o = o.reshape(B, L, GLA_VAL) * jax.nn.silu(og.astype(f32))
    return o.astype(q.dtype), s_f, s_b

def peer_ffn(h, wq, sub_keys, u_tab, v_tab):
    f32 = jnp.float32
    B, L, D = h.shape
    T = B * L
    x = h.reshape(T, D)
    q = (x @ wq).reshape(T, PEER_HEADS, 2, PEER_DQ // 2).astype(f32)
    s = jnp.einsum('thpd,hpkd->thpk', q, sub_keys.astype(f32))
    s_top, i_top = lax.top_k(s, PEER_TOPK)
    cand_s = (s_top[:, :, 0, :, None] + s_top[:, :, 1, None, :]).reshape(T, PEER_HEADS, -1)
    cand_i = (i_top[:, :, 0, :, None] * PEER_NKEYS + i_top[:, :, 1, None, :]).reshape(T, PEER_HEADS, -1)
    best, pos = lax.top_k(cand_s, PEER_TOPK)
    idx = jnp.take_along_axis(cand_i, pos, axis=-1)
    gate = jax.nn.softmax(best, axis=-1)
    nb = T // PEER_BLOCK
    xb = x.reshape(nb, PEER_BLOCK, D)
    ib = idx.reshape(nb, PEER_BLOCK, PEER_HEADS * PEER_TOPK)
    gb = gate.reshape(nb, PEER_BLOCK, PEER_HEADS * PEER_TOPK).astype(h.dtype)

    def block(args):
        xt, it, gt = args
        a = jax.nn.gelu(jnp.einsum('td,tkd->tk', xt, u_tab[it]))
        return jnp.einsum('tk,tkd->td', gt * a, v_tab[it])

    y = lax.map(block, (xb, ib, gb))
    return y.reshape(B, L, D)

def trunk_layer(x, mod, s0_f, s0_b, row_len, lw):
    sh1, sc1, g1, sh2, sc2, g2 = jnp.split(mod[:, None, :].astype(x.dtype), 6, axis=-1)
    h = rms_norm(x, lw['norm_pre1']) * (1 + sc1) + sh1
    proj = h @ lw['w_in']
    o0 = 3 * HY_CH
    cuts = [o0, o0 + GLA_KEY, o0 + 2 * GLA_KEY, o0 + 2 * GLA_KEY + GLA_VAL, o0 + 2 * GLA_KEY + 2 * GLA_VAL]
    hy, q, k, v, og, lr = jnp.split(proj, cuts, axis=-1)
    y_hy = hyena_mix(hy, row_len, lw['hy_conv_w'], lw['hy_conv_b'], lw['hf_w1'], lw['hf_b1'],
                     lw['hf_w2'], lw['hf_b2'], lw['hf_w3'], lw['hf_freq'], lw['hy_bias'])
    y_gla, s_f, s_b = gla_mix(q, k, v, og, lr, s0_f, s0_b, lw['gla_w2_f'], lw['gla_b_f'],
                              lw['gla_w2_b'], lw['gla_b_b'], lw['gla_norm'])
    mix = jnp.concatenate([y_hy, y_gla], axis=-1) @ lw['w_out']
    x = x + g1 * rms_norm(mix, lw['norm_post1'])
    h2 = rms_norm(x, lw['norm_pre2']) * (1 + sc2) + sh2
    ff = peer_ffn(h2, lw['peer_wq'], lw['peer_keys'], lw['peer_u'], lw['peer_v'])
    x = x + g2 * rms_norm(ff, lw['norm_post2'])
    return x, s_f, s_b

def setup_inputs(seed: int = 0) -> dict:
    key = jax.random.key(seed)
    ks = jax.random.split(key, 32)
    nrm = jax.random.normal
    D = D_MODEL
    return {
        'x_prompt': nrm(ks[0], (BATCH, SEQ, D), jnp.float32),
        'x_sample': nrm(ks[1], (DEC_BATCH, DEC_SEQ, D), jnp.float32),
        'state_gla': 0.5 * nrm(ks[2], (DEC_BATCH, DEPTH, 2, GLA_HEADS, GLA_DK, GLA_DV), jnp.float32),
        'c': nrm(ks[3], (DEC_BATCH, D), jnp.float32),
        'c_ctx': nrm(ks[4], (D,), jnp.float32),
        'w_ada': 0.5 * D ** -0.5 * nrm(ks[5], (DEPTH, D, 6 * D), jnp.float32),
        'b_ada': 0.02 * nrm(ks[6], (DEPTH, 6 * D), jnp.float32),
        'norm_pre1': 1.0 + 0.05 * nrm(ks[7], (DEPTH, D), jnp.float32),
        'norm_post1': 1.0 + 0.05 * nrm(ks[8], (DEPTH, D), jnp.float32),
        'norm_pre2': 1.0 + 0.05 * nrm(ks[9], (DEPTH, D), jnp.float32),
        'norm_post2': 1.0 + 0.05 * nrm(ks[10], (DEPTH, D), jnp.float32),
        'w_in': D ** -0.5 * nrm(ks[11], (DEPTH, D, IN_COLS), jnp.float32),
        'hy_conv_w': HY_SHORT ** -0.5 * nrm(ks[12], (DEPTH, HY_SHORT, 3 * HY_CH), jnp.float32),
        'hy_conv_b': 0.02 * nrm(ks[13], (DEPTH, 3 * HY_CH), jnp.float32),
        'hf_w1': HY_EMB ** -0.5 * nrm(ks[14], (DEPTH, HY_EMB, HY_FILT_HID), jnp.float32),
        'hf_b1': 0.1 * nrm(ks[15], (DEPTH, HY_FILT_HID), jnp.float32),
        'hf_w2': HY_FILT_HID ** -0.5 * nrm(ks[16], (DEPTH, HY_FILT_HID, HY_FILT_HID), jnp.float32),
        'hf_b2': 0.1 * nrm(ks[17], (DEPTH, HY_FILT_HID), jnp.float32),
        'hf_w3': 0.05 * nrm(ks[18], (DEPTH, HY_FILT_HID, 2 * HY_CH), jnp.float32),
        'hf_freq': 1.0 + 0.05 * nrm(ks[19], (DEPTH, HY_FILT_HID), jnp.float32),
        'hy_bias': 0.1 * nrm(ks[20], (DEPTH, HY_CH), jnp.float32),
        'gla_w2_f': GLA_RANK ** -0.5 * nrm(ks[21], (DEPTH, GLA_RANK, GLA_KEY), jnp.float32),
        'gla_b_f': 0.1 * nrm(ks[22], (DEPTH, GLA_KEY), jnp.float32),
        'gla_w2_b': GLA_RANK ** -0.5 * nrm(ks[23], (DEPTH, GLA_RANK, GLA_KEY), jnp.float32),
        'gla_b_b': 0.1 * nrm(ks[24], (DEPTH, GLA_KEY), jnp.float32),
        'gla_norm': 1.0 + 0.05 * nrm(ks[25], (DEPTH, GLA_DV), jnp.float32),
        'w_out': MIX_W ** -0.5 * nrm(ks[26], (DEPTH, MIX_W, D), jnp.float32),
        'peer_wq': D ** -0.5 * nrm(ks[27], (DEPTH, D, PEER_HEADS * PEER_DQ), jnp.float32),
        'peer_keys': (PEER_DQ // 2) ** -0.5 * nrm(ks[28], (DEPTH, PEER_HEADS, 2, PEER_NKEYS, PEER_DQ // 2), jnp.float32),
        'peer_u': D ** -0.5 * nrm(ks[29], (DEPTH, PEER_EXPERTS, D), jnp.float32),
        'peer_v': (PEER_HEADS * PEER_TOPK) ** -0.5 * nrm(ks[30], (DEPTH, PEER_EXPERTS, D), jnp.float32),
    }

def reference(x_prompt, x_sample, state_gla, c, c_ctx, w_ada, b_ada, norm_pre1, norm_post1,
              norm_pre2, norm_post2, w_in, hy_conv_w, hy_conv_b, hf_w1, hf_b1, hf_w2, hf_b2,
              hf_w3, hf_freq, hy_bias, gla_w2_f, gla_b_f, gla_w2_b, gla_b_b, gla_norm, w_out,
              peer_wq, peer_keys, peer_u, peer_v):
    xp = x_prompt
    xs = x_sample
    ctx_states = []
    for l in range(DEPTH):
        lw = {
            'norm_pre1': norm_pre1[l], 'norm_post1': norm_post1[l],
            'norm_pre2': norm_pre2[l], 'norm_post2': norm_post2[l],
            'w_in': w_in[l], 'hy_conv_w': hy_conv_w[l], 'hy_conv_b': hy_conv_b[l],
            'hf_w1': hf_w1[l], 'hf_b1': hf_b1[l], 'hf_w2': hf_w2[l], 'hf_b2': hf_b2[l],
            'hf_w3': hf_w3[l], 'hf_freq': hf_freq[l], 'hy_bias': hy_bias[l],
            'gla_w2_f': gla_w2_f[l], 'gla_b_f': gla_b_f[l], 'gla_w2_b': gla_w2_b[l],
            'gla_b_b': gla_b_b[l], 'gla_norm': gla_norm[l], 'w_out': w_out[l],
            'peer_wq': peer_wq[l], 'peer_keys': peer_keys[l], 'peer_u': peer_u[l], 'peer_v': peer_v[l],
        }
        mod_ctx = (jax.nn.silu(c_ctx) @ w_ada[l] + b_ada[l])[None, :]
        mod_lat = jax.nn.silu(c) @ w_ada[l] + b_ada[l]
        z0 = jnp.zeros((xp.shape[0], GLA_HEADS, GLA_DK, GLA_DV), jnp.float32)
        xp, s_f, s_b = trunk_layer(xp, mod_ctx, z0, z0, xp.shape[1], lw)
        ctx_states.append(jnp.stack([s_f, s_b], axis=1))
        st = state_gla[:, l].astype(jnp.float32)
        xs, _, _ = trunk_layer(xs, mod_lat, st[:, 0], st[:, 1], GRID_W, lw)
    new_state_gla = jnp.stack(ctx_states, axis=1).astype(x_prompt.dtype)
    return (xp, xs, new_state_gla)


_drawn_inputs = setup_inputs


def setup_inputs(seed=0):
    import zlib

    import numpy as np

    out = dict(_drawn_inputs(seed))
    spreads = {}
    factors = {'state_gla': 7.118, 'norm_post2': 4.089}
    for name, (base, spread) in spreads.items():
        noise = np.random.default_rng([zlib.crc32(name.encode()), seed]).standard_normal(out[name].shape)
        drawn = base * np.exp(spread * noise) if base else spread * noise
        out[name] = __import__('jax').numpy.asarray(drawn.astype(out[name].dtype))
    for name, factor in factors.items():
        out[name] = (out[name] * factor).astype(out[name].dtype)
    return out
```

```python
import math
from contextlib import ExitStack

import numpy as np

import concourse.bass as bass
from concourse import mybir

ALU = mybir.AluOpType
ACT = mybir.ActivationFunctionType
AX_X = mybir.AxisListType.X
F32 = mybir.dt.float32
F32R = mybir.dt.float32r
U32 = mybir.dt.uint32
BF16 = mybir.dt.bfloat16

P = 128
D = 1024
KD = D // P
LP, LS = 128, 512
T = LP + LS
TH = T // 2
NT = T // P
HY = 512
CT = HY // P
SHORT = 3
ROW = 64
EMB, HID = 33, 64
DK, DV, HEADS = 64, 128, 4
RANK = 16
GATE_NORM = 16.0
EPS = 1e-6
W_V, W_OG, W_QK, W_LR = 2048, 2560, 1536, 3072
PH, NKEYS, TOPK = 8, 128, 16
HP = 2 * PH
HK = PH * TOPK
NBLK = 128
KiB = 1024
NEG = -3.0e38

C_BADA = 0
C_PRE1 = C_BADA + 6 * KD
C_PRE2 = C_PRE1 + KD
C_POST1 = C_PRE2 + KD
C_POST2 = C_POST1 + KD
C_CW = C_POST2 + KD
C_CB = C_CW + SHORT * 3 * CT
C_HB = C_CB + 3 * CT
C_GB = C_HB + CT
C_ALL = C_GB + 4

NADA, NHYB = 12, 6
BLK_A = 48
TOK_BLK = 8
RING = 8
GRP = 4


MIX_ORDER = [("mix", 0), ("mix", 1), ("mix", 2), ("turn", 0), ("mix", 3), ("turn", 1), ("mix", 4), ("turn", 2),
             ("turn", 3), ("turn", 4)]
KV_ORDER = [(0, "f"), (0, "b"), (1, "f"), (4, "b"), (2, "f"), (3, "b"), (3, "f"), (2, "b")]


def seq_of(tile):
    return 0 if tile == 0 else 1


def bass_hybrid_layer(nc, x, cvec, w_ada, w_in, w_out, w_q, cols, hfcols, hf_w1, hf_w2, hf_w3,
                      gla_w2, gnorm, state, keys_t, u_t, v_tab, zfeat, decay, tab_fwd, tab_inv, tab_p,
                      masks, ident_d, iota_d, out, out_state):
    a_dram = nc.dram_tensor("gelu_scratch", [NBLK, P, T], F32, kind="Internal").ap()
    g_dram = nc.dram_tensor("gate_scratch", [NBLK, P, T], F32, kind="Internal").ap()

    ctx = ExitStack()
    with ctx:
        base = 17 * KiB

        def at(name, kib, shape, dt=F32):
            return nc.alloc_sbuf_tensor_at(name, shape, dt, offset=int(base + kib * KiB))

        def sem(name):
            return ctx.enter_context(nc.semaphore(name))

        x_sb = at("x_sb", 0, [P, NT, D])
        v_sb = at("v_sb", 0, [P, NT, 512])
        og_sb = at("og_sb", 10, [P, NT, 512])
        g2row = at("g2row", 20, [P, 2, D])
        g1row = at("g1row", 28, [P, 2, D])
        tab = at("tab", 20, [P, 4, 2, 512])
        hT = at("hT", 40, [P, KD, T])
        h2lo = at("h2lo", 40, [P, KD, T], F32R)
        mixT = at("mixT", 60, [P, KD, T])
        h2hi = at("h2hi", 60, [P, KD, T], F32R)
        wring = at("wring", 80, [P, 3, KD, 512])
        x0 = at("x0", 128, [P, CT, T])
        z = at("z", 138, [P, CT, T])
        x1 = at("x1", 148, [P, CT, T])
        zt = at("zt", 148, [P, NT, 512])
        kp = at("kp", 158, [P, NT, 512])
        km = at("km", 168, [P, NT, 512])
        Yc = at("Yc", 158, [P, NT, 512])
        Yn = at("Yn", 168, [P, NT, 512])
        Kcs = at("Kcs", 178, [P, NT, 2, 512])
        dec_sb = at("dec_sb", 178, [P, NT, 512])
        fh = at("fh", 188, [HID, 2, T])
        fw3 = at("fw3", 193, [HID, 2 * HY])
        Kscr = at("Kscr", 76, [P, D])
        ytmp = at("ytmp", 60 + 12, [P, 2, 512])
        qk = at("qk", 128, [P, 4, T])
        la = at("la", 138, [P, 4, T])
        bc = at("bc", 148, [P, 4, T])
        eq = at("eq", 158, [P, 4, T])
        ek = at("ek", 168, [P, 4, T])
        keT = at("keT", 178, [P, NT, 4, 128])
        am = at("am", 138, [P, 2, 2, 512])
        s_cur = at("s_cur", 188, [P, 2, 2, 128])
        spd = at("spd", 20, [P, 2, 4, 2, 2, 128])
        o_sb = at("o_sb", 148, [P, NT, 512])
        osq = at("osq", 168, [P, NT, 512])
        lr_sb = at("lr_sb", 178, [RANK, 2, T])
        mix_sb = at("mix_sb", 148, [P, NT, D])
        diag = at("diag", 168, [P, 2, 512])
        sq_scr = at("sq_scr", 172, [P, D])
        h2T = at("h2T", 128, [P, KD, T])
        scores = at("scores", 148, [P, NT, HP, NKEYS])
        keysT = at("keysT", 188, [P, HP, NKEYS])
        qbuf = at("qbuf", 28, [P, 2, T])
        qwhi = at("qwhi", 128, [P, 2, KD, 128], F32R)
        qwlo = at("qwlo", 136, [P, 2, KD, 128], F32R)
        srep = at("srep", 128, [P, NKEYS])
        crep = at("crep", 128.5, [P, 256])
        cand = at("cand", 129.5, [P, PH, 16, 16])
        oneh = at("oneh", 137.5, [P, HK, 16])
        cols_hk = at("cols_hk", 28, [P, 4, T])
        uraw = at("uraw", 80, [P, 4, KD, 128])
        uhi = at("uhi", 96, [P, 2, KD, 128], F32R)
        ulo = at("ulo", 104, [P, 2, KD, 128], F32R)
        aout = at("aout", 112, [P, 4, T])
        eB = at("eB", 122, [P, RING, 128], BF16)
        eA = at("eA", 124, [P, 3, RING, 128], BF16)
        g3col = at("g3col", 130, [P, T])
        iota_b = at("iota_b", 132.5, [P, 128], BF16)
        part = at("part", 133, [P, 2, 128], BF16)
        rest = at("rest", 133.5, [P, 128])
        gst = at("gst", 139, [P, 2, 128, 64])
        yacc = at("yacc", 28, [P, NT, D])
        whi = at("whi", 48, [P, 2, GRP, T], F32R)
        wlo = at("wlo", 68, [P, 2, GRP, T], F32R)
        vhi = at("vhi", 88, [P, 2, GRP, D], F32R)
        vlo = at("vlo", 120, [P, 2, GRP, D], F32R)
        vraw = at("vraw", 152, [P, 4, D])
        ain = at("ain", 168, [P, 4, T])
        gin = at("gin", 178, [P, 4, T])
        place = [203 * KiB]

        def small(name, shape, dt=F32):
            n = int(np.prod(shape[1:])) * 4
            t = nc.alloc_sbuf_tensor_at(name, shape, dt, offset=base + place[0])
            place[0] += (n + 31) // 32 * 32
            return t

        ident = small("ident", [P, 128])
        iota = small("iota", [P, 128])
        colv = small("colv", [P, C_ALL])
        mod = small("mod", [P, 6 * KD, 2])
        scale1 = small("scale1", [P, KD, 2])
        scale2 = small("scale2", [P, KD, 2])
        gcol = small("gcol", [P, 2, KD, 2])
        cs = small("cs", [P, KD, 2])
        cin = small("cin", [P, KD, 2])
        stat = small("stat", [P, 4, 24])
        er = small("er", [P, 4, NT])
        ones_m = small("ones_m", [P, 128])
        assert base + place[0] <= 229344, place
        w_lr = at("w_lr", 198, [P, KD, 2 * RANK])
        tabp = at("tabp", 199, [P, 4, 128])
        hbend = at("hbend", 201, [P, 4, NT])
        mask = at("mask", 201.25, [P, 2, 128])
        hfc = at("hfc", 202.25, [HID, 3])
        fw1 = at("fw1", 197, [EMB, HID])
        fw2 = at("fw2", 197.5, [HID, HID])
        modrow = at("modrow", 36, [2, 2, 512])
        zf = at("zf", 60, [EMB, T])
        ft = at("ft", 64, [HID, 2, T])
        gw2 = at("gw2", 183, [RANK, 512])
        gnrow = at("gnrow", 202.5, [P, 128])
        st_out = at("st_out", 36, [P, 2, 2, 128])
        sval = at("sval", 28 + 10.5, [P, HP, 16])
        sidx = at("sidx", 128 - 1, [P, HP, 16], U32)
        selw = at("selw", 188, [P, NT, 3, HK])
        work = at("work", 198, [P, 6, HK])
        itopf = at("itopf", 201, [P, HP, 16])

        ps = ctx.enter_context(nc.psum_tensor("ps", [P, 8, 512], F32))

        order = ["fa_p", "fa_s", "fb_p", "fb_s"]
        order += [f"fc{t}{d}" for t in range(NT) for d in "fb"]
        for i in range(4):
            order += [f"ada{i}"] + ([f"adc{i - 1}"] if i else [])
        order += ["adc3"]
        order += ["tr1_p0", "tr1_p1"] + [f"tr1_{k}" for k in range(KD)]
        order += [f"hy{c}{s}" for c in range(3 * CT) for s in "ps"]
        order += [f"kd{f}{d}" for f in range(NT) for d in "cs"]
        order += [f"v{t}" for t in range(NT)]
        order += [f"zt{t}" for t in range(NT)]
        order += [f"zd{f}{d}" for f in range(NT) for d in "cs"]
        order += [f"og{t}" for t in range(NT)]
        order += [f"yi{c}{s}" for c in range(CT) for s in "ps"]
        order += [f"lr{d}{s}" for d in "fb" for s in "ps"]
        order += [f"qk{c}{s}" for c in range(4) for s in "ps"]
        order += [f"la{j}{s}" for j in range(4) for s in "ps"]
        for i in range(4, NADA):
            order += [f"ada{i}"] + ([f"adc{i - 1}"] if i > 4 else [])
        order += [f"adc{NADA - 1}"]
        order += [f"kT{c}" for c in range(NT)]
        order += [f"kv{c}{d}" for c, d in KV_ORDER]
        for c in range(NT):
            order += [f"at{c}0", f"at{c}1"] + ([f"o{c - 1}"] if c else [])
        order += [f"o{NT - 1}"]
        order += [f"gr{g}{s}{h}" for g in range(2) for s in range(2) for h in range(2)]
        order += [f"ot{c}" for c in range(NT)]
        for kind, t in MIX_ORDER:
            order += [f"mx0{t}", f"mx1{t}"] if kind == "mix" else [f"tr2_{t}0", f"tr2_{t}1"]
        for h in range(HP):
            order += [f"q{h}p", f"q{h}s"]
            if h:
                order += [f"sc{h-1}p", f"sc{h-1}s"]
        order += [f"sc{HP-1}p", f"sc{HP-1}s"]
        unit = {u: n for n, u in enumerate(order)}
        assert len(unit) == len(order)

        bank_full = sem("bank_full")
        drained = [sem(f"drained{b}") for b in range(8)]

        def bank(u, a=0, b=512):
            return ps[:, unit[u] % 8, a:b]

        def wait_bank_free(eng, u):
            if unit[u] >= 8:
                eng.wait_ge(drained[unit[u] % 8], unit[u] // 8)

        def wait_unit(eng, u):
            eng.wait_ge(bank_full, unit[u] + 1)

        def drain_of(u):
            return drained[unit[u] % 8]

        def wait_drained(eng, u):
            eng.wait_ge(drained[unit[u] % 8], unit[u] // 8 + 1)

        ld_small = sem("ld_small")
        ld_filt = sem("ld_filt")
        ld_dec = sem("ld_dec")
        ld_x = sem("ld_x")
        ld_tab = sem("ld_tab")
        ld_tabi = sem("ld_tabi")
        ld_lr = sem("ld_lr")
        ld_gw = sem("ld_gw")
        ld_state = sem("ld_state")
        ld_xr = sem("ld_xr")
        ld_keys = sem("ld_keys")
        w_landed = [sem(f"w_landed{i}") for i in range(3)]
        const_ready = sem("const_ready")
        cs_ready = sem("cs_ready")
        modrow_ready = sem("modrow_ready")
        f_arg = sem("f_arg")
        f_sin = sem("f_sin")
        kpm_ready = sem("kpm_ready")
        ssq1 = sem("ssq1")
        ms1 = sem("ms1")
        rt1 = sem("rt1")
        xn_ready = sem("xn_ready")
        z_ready = sem("z_ready")
        hyc1 = sem("hyc1")
        y_ready = sem("y_ready")
        hy_done = sem("hy_done")
        ax_ready = sem("ax_ready")
        ln_done = sem("ln_done")
        hb_ready = sem("hb_ready")
        bc_ready = sem("bc_ready")
        er_ready = sem("er_ready")
        exp_done = sem("exp_done")
        qe_ready = sem("qe_ready")
        am_ready = sem("am_ready")
        am_used = sem("am_used")
        sp_ready = sem("sp_ready")
        spd_zero = sem("spd_zero")
        st_out_ready = sem("st_out_ready")
        o_ms = sem("o_ms")
        o_rt = sem("o_rt")
        o_ready = sem("o_ready")
        gate_ready = sem("gate_ready")
        diag_ready = sem("diag_ready")
        mix_ssq = sem("mix_ssq")
        mix_ms = sem("mix_ms")
        mix_rt = sem("mix_rt")
        x1_ready = sem("x1_ready")
        x1_ssq = sem("x1_ssq")
        x1_ms = sem("x1_ms")
        x1_rt = sem("x1_rt")
        xn2_ready = sem("xn2_ready")
        h2_ready = sem("h2_ready")
        h2hi_ready = sem("h2hi_ready")
        h2lo_ready = sem("h2lo_ready")
        qwhi_ready = sem("qwhi_ready")
        qwlo_ready = sem("qwlo_ready")
        st_done = sem("st_done")
        seq_dve = sem("seq_dve")
        seq_act = sem("seq_act")

        loads = []
        loads += [("ada", i) for i in range(4)] + [("in", 0), ("in", 512), ("in", 1024), ("in", W_V),
                                                   ("in", W_OG), ("in", W_QK)]
        loads += [("ada", i) for i in range(4, NADA)] + [("out", 0), ("out", 512)]
        loads += [("q", 512 * i) for i in range(4)]
        wslot = {l: n for n, l in enumerate(loads)}

        def last_unit(l):
            kind, i = l
            if kind == "ada":
                return f"ada{i}"
            if kind == "out":
                return f"mx{i // 512}{NT - 1}"
            if kind == "q":
                return f"q{i // P + 3}s"
            return {0: "hy3s", 512: "hy7s", 1024: "hy11s", W_V: f"v{NT - 1}", W_OG: f"og{NT - 1}", W_QK: "qk3s"}[i]

        def wtile(l):
            return wring[:, wslot[l] % 3]

        def wait_w(eng, l):
            eng.wait_ge(w_landed[wslot[l] % 3], 16 * (wslot[l] // 3 + 1))

        scols = slice(LP, T)

        def seq_cols(s):
            return (0, LP) if s == "p" else (LP, T)
        g_stored = [sem(f"g_stored{b}") for b in range(2)]
        a_stored = [sem(f"a_stored{b}") for b in range(4)]
        u_landed = [sem(f"u_landed{b}") for b in range(4)]
        uhi_ready = sem("uhi_ready")
        ulo_ready = sem("ulo_ready")
        h_full = sem("h_full")
        gelu_done = sem("gelu_done")
        topk_exp_in = sem("topk_exp_in")
        topk_exp = sem("topk_exp")
        sel_ready = sem("sel_ready")
        cl_full = sem("cl_full")
        cl_drained = sem("cl_drained")
        onehot_ready = sem("onehot_ready")
        onehot_used = sem("onehot_used")
        gate_full = sem("gate_full")
        gate_staged = sem("gate_staged")
        v_landed = [sem(f"v_landed{b}") for b in range(4)]
        a_landed = [sem(f"a_landed{b}") for b in range(4)]
        g_landed = [sem(f"g_landed{b}") for b in range(4)]
        vhi_ready = sem("vhi_ready")
        vlo_ready = sem("vlo_ready")
        w_ready = sem("w_ready")
        whi_ready = sem("whi_ready")
        wlo_ready = sem("wlo_ready")
        y_full = sem("y_full")
        y_added = sem("y_added")
        yacc_clear = sem("yacc_clear")
        pass1_in = sem("pass1_in")
        y_ssq = sem("y_ssq")
        y_ms = sem("y_ms")
        y_rt = sem("y_rt")
        y_fin = sem("y_fin")
        stored = sem("stored")

        NU = len(order)
        NB_BODY_A, NB_BODY_B = 4, 2 * 64 // TOK_BLK
        IT_A, IT_B = BLK_A // NB_BODY_A, (NBLK - BLK_A) // NB_BODY_B
        assert IT_B * 2 * 64 == T
        IT_2 = NBLK // (2 * GRP)

        def loop(eng, n, body, *more):
            body(0, True, *more)
            with eng.Fori(1, n) as it:
                body(it, False, *more)

        block = ctx.enter_context(nc.Block())

        @block.sync
        def _(sp_):
            def small_load(dst, src, s):
                sp_.dma_start(dst, src).then_inc(s, 16)

            small_load(colv[:], cols, ld_small)
            small_load(ident[:], ident_d, ld_small)
            small_load(cin[:], cvec, ld_small)
            small_load(hfc[:], hfcols, ld_filt)
            small_load(zf[:], zfeat, ld_filt)
            small_load(fw1[:], hf_w1, ld_filt)
            small_load(fw2[:], hf_w2, ld_filt)
            small_load(fw3[:], hf_w3, ld_filt)

            def load_w(l):
                kind, i = l
                n = wslot[l]
                if n >= 3:
                    wait_unit(sp_, last_unit(loads[n - 3]))
                src, c0 = {"ada": (w_ada, 512 * i), "in": (w_in, i), "out": (w_out, i), "q": (w_q, i)}[kind]
                sp_.dma_start(wtile(l), src.rearrange("(k p) n -> p k n", p=P)[:, :, c0:c0 + 512]
                              ).then_inc(w_landed[n % 3], 16)

            load_w(loads[0])
            small_load(x_sb[:], x.rearrange("(t p) d -> p t d", p=P), ld_x)
            small_load(dec_sb[:], decay, ld_dec)
            for l in loads[1:5]:
                load_w(l)
            small_load(tab[:], tab_fwd, ld_tab)
            small_load(tabp[:], tab_p, ld_tab)
            small_load(w_lr[:], w_in.rearrange("(k p) n -> p k n", p=P)[:, :, W_LR:W_LR + 2 * RANK], ld_lr)
            small_load(mask[:], masks, ld_lr)
            small_load(gnrow[:], gnorm.rearrange("(o e) -> o e", o=1).broadcast_to([P, DV]), ld_lr)
            small_load(iota[:], iota_d, ld_lr)
            for l in loads[5:11]:
                load_w(l)
            wait_unit(sp_, f"zd{NT - 1}s")
            small_load(tab[:], tab_inv, ld_tabi)
            sp_.wait_ge(y_ready, NT)
            small_load(gw2[:], gla_w2, ld_gw)
            small_load(s_cur[:], state, ld_state)
            for l in loads[11:21]:
                load_w(l)
            sp_.wait_ge(o_ready, NT)
            small_load(x_sb[:], x.rearrange("(t p) d -> p t d", p=P), ld_xr)
            small_load(keysT[:], keys_t, ld_keys)
            sp_.wait_ge(st_out_ready, 2)
            small_load(out_state.rearrange("o r (k h) d e -> (o h d) r k e", h=2), st_out[:], stored)
            for l in loads[21:]:
                load_w(l)

            def load_u(n, slot):
                sp_.dma_start(uraw[:, slot], u_t[bass.ds(n, 1)].rearrange("o p k e -> p (o k) e")
                              ).then_inc(u_landed[slot], 16)

            def store_a(n, slot):
                sp_.wait_ge(gelu_done, n + 1)
                sp_.dma_start(a_dram[bass.ds(n, 1)].rearrange("o p t -> p (o t)"), aout[:, slot]
                              ).then_inc(a_stored[slot], 16)

            wait_unit(sp_, last_unit(loads[-1]))
            for n in range(4):
                load_u(n, n)

            def step_a(it, first, b0, nb, last):
                for b in range(nb):
                    n = it * nb + b + b0
                    store_a(n, b % 4)
                    if not last:
                        sp_.wait_ge(uhi_ready, n + 1)
                        sp_.wait_ge(ulo_ready, n + 1)
                        load_u(n + 4, b % 4)

            loop(sp_, IT_A, lambda it, first: step_a(it, first, 0, NB_BODY_A, False))

            def step_b(it):
                for b in range(NB_BODY_B):
                    n = it * NB_BODY_B + b + BLK_A
                    store_a(n, b % 4)
                    sp_.wait_ge(uhi_ready, n + 1)
                    sp_.wait_ge(ulo_ready, n + 1)
                    if not (isinstance(it, int) and n + 4 >= NBLK):
                        load_u(n + 4, b % 4)
                    if b % 8 == 7:
                        half = b // 8
                        sp_.wait_ge(gate_staged, it * 32 + 16 * (half + 1))
                        sp_.dma_start(g_dram.rearrange("i p (c t) -> c p i t", t=64)[
                            bass.ds(it * 2 + half, 1)].rearrange("o p i t -> (o p) i t"), gst[:, half]
                            ).then_inc(g_stored[half], 16)

            step_b(0)
            with sp_.Fori(1, IT_B - 1) as it:
                step_b(it)
            step_b(IT_B - 1)

            for b in range(4):
                sp_.wait_ge(a_stored[b], 16 * (NBLK // 4))
            for b in range(2):
                sp_.wait_ge(g_stored[b], 16 * IT_B)

            def step_2(it, first):
                for b in range(2 * GRP):
                    n = it * 2 * GRP + b
                    s = b % 4
                    if not first or b >= 4:
                        sp_.wait_ge(vhi_ready, n - 3)
                        sp_.wait_ge(vlo_ready, n - 3)
                    sp_.dma_start(vraw[:, s], v_tab.rearrange("(i p) d -> i p d", p=P)[bass.ds(n, 1)]
                                  .rearrange("o p d -> (o p) d")).then_inc(v_landed[s], 16)
                    if not first or b >= 4:
                        sp_.wait_ge(whi_ready, n - 3)
                        sp_.wait_ge(wlo_ready, n - 3)
                    sp_.dma_start(ain[:, s], a_dram[bass.ds(n, 1)].rearrange("o p t -> p (o t)")
                                  ).then_inc(a_landed[s], 16)
                    sp_.dma_start(gin[:, s], g_dram[bass.ds(n, 1)].rearrange("o p t -> p (o t)")
                                  ).then_inc(g_landed[s], 16)

            loop(sp_, IT_2, step_2)
            for t in range(NT):
                sp_.wait_ge(y_fin, t + 1)
                sp_.dma_start(out[t * P:(t + 1) * P, :], yacc[:, t]).then_inc(stored, 16)
            sp_.wait_ge(stored, 16 * (NT + 1))

        @block.tensor
        def _(pe):
            def rows(t):
                return slice(t * P, (t + 1) * P)

            def transposes(u, pieces):
                wait_bank_free(pe, u)
                for j, a in enumerate(pieces):
                    last = pe.transpose(bank(u, j * P, (j + 1) * P), a, ident[:])
                last.then_inc(bank_full, 1)

            def both(up, us, m, pieces, wait=None):
                wait_bank_free(pe, up)
                wait_bank_free(pe, us)
                n = len(pieces)
                for j, (w, ap, as_) in enumerate(pieces):
                    p_ = pe.matmul(bank(up, 0, LP)[0:m], w, ap, start=(j == 0), stop=(j == n - 1))
                    s_ = pe.matmul(bank(us)[0:m], w, as_, start=(j == 0), stop=(j == n - 1))
                    if j == n - 1:
                        p_.then_inc(bank_full, 1)
                s_.then_inc(bank_full, 1)

            pe.wait_ge(ld_filt, 16 * 5)
            both("fa_p", "fa_s", HID, [(fw1[:], zf[:, 0:LP], zf[:, LP:T])])
            pe.wait_ge(f_sin, 1)
            both("fb_p", "fb_s", HID, [(fw2[:], fh[:, 0, 0:LP], fh[:, 0, LP:T])])
            pe.wait_ge(f_sin, 2)
            for t in range(NT):
                for j, d in enumerate("fb"):
                    u = f"fc{t}{d}"
                    wait_bank_free(pe, u)
                    pe.matmul(bank(u), fh[:, 1, rows(t)], fw3[:, j * HY:(j + 1) * HY], start=True, stop=True
                              ).then_inc(bank_full, 1)

            def ada(i):
                u = f"ada{i}"
                wait_w(pe, ("ada", i))
                wait_bank_free(pe, u)
                for k in range(KD):
                    last = pe.matmul(bank(u)[0:2], cs[:, k, :], wtile(("ada", i))[:, k, :], start=(k == 0), stop=(k == KD - 1))
                last.then_inc(bank_full, 1)

            def ada_cols(i):
                u = f"adc{i}"
                pe.wait_ge(modrow_ready, i + 1)
                wait_bank_free(pe, u)
                for c in range(4):
                    last = pe.transpose(bank(u, 2 * c, 2 * c + 2), modrow[:, i % 2, c * P:(c + 1) * P], ident[0:2, 0:2])
                last.then_inc(bank_full, 1)

            def modulations(i0, i1):
                for i in range(i0, i1):
                    ada(i)
                    if i > i0:
                        ada_cols(i - 1)
                ada_cols(i1 - 1)

            pe.wait_ge(cs_ready, 1)
            pe.wait_ge(ld_small, 16 * 3)
            modulations(0, 4)

            pe.wait_ge(ld_small, 16 * 3)
            pe.wait_ge(xn_ready, NT)
            for h in range(2):
                transposes(f"tr1_p{h}", [x_sb[:, 0, (4 * h + j) * P:(4 * h + j + 1) * P] for j in range(4)])
            for k in range(KD):
                transposes(f"tr1_{k}", [x_sb[:, t, k * P:(k + 1) * P] for t in range(1, NT)])
            for k in range(KD):
                wait_drained(pe, f"tr1_{k}")

            for c in range(3 * CT):
                l = ("in", 512 * (c // 4))
                if c % 4 == 0:
                    wait_w(pe, l)
                both(f"hy{c}p", f"hy{c}s", P,
                     [(wtile(l)[:, k, (c % 4) * P:(c % 4 + 1) * P], hT[:, k, 0:LP], hT[:, k, LP:T]) for k in range(KD)])
            pe.wait_ge(ld_tab, 32)
            pe.wait_ge(kpm_ready, NT)

            def spectrum(name, a_c, a_s):
                for f in range(NT):
                    for j, (d, a) in enumerate((("c", a_c), ("s", a_s))):
                        u = f"{name}{f}{d}"
                        wait_bank_free(pe, u)
                        if f == 0:
                            last = pe.matmul(bank(u), tabp[:, j], a(0), start=True, stop=True)
                        else:
                            for t in range(4):
                                last = pe.matmul(bank(u), tab[:, t, j, (f - 1) * P:f * P], a(1 + t),
                                                 start=(t == 0), stop=(t == 3))
                        last.then_inc(bank_full, 1)

            spectrum("kd", lambda t: kp[:, t], lambda t: km[:, t])
            def by_token(name, l):
                wait_w(pe, l)
                for t in range(NT):
                    u = f"{name}{t}"
                    wait_bank_free(pe, u)
                    for k in range(KD):
                        last = pe.matmul(bank(u), hT[:, k, rows(t)], wtile(l)[:, k, :], start=(k == 0), stop=(k == KD - 1))
                    last.then_inc(bank_full, 1)

            by_token("v", ("in", W_V))
            pe.wait_ge(z_ready, CT)
            for t in range(NT):
                transposes(f"zt{t}", [z[:, c, rows(t)] for c in range(CT)])
            for t in range(NT):
                wait_drained(pe, f"zt{t}")
            spectrum("zd", lambda t: zt[:, t], lambda t: zt[:, t])
            by_token("og", ("in", W_OG))
            pe.wait_ge(y_ready, NT)
            pe.wait_ge(ld_tabi, 16)
            for c in range(CT):
                cc = slice(c * P, (c + 1) * P)
                up, us = f"yi{c}p", f"yi{c}s"
                wait_bank_free(pe, up)
                pe.matmul(bank(up, 0, LP), Yc[:, 0, cc], tabp[:, 2], start=True, stop=False)
                pe.matmul(bank(up, 0, LP), Yn[:, 0, cc], tabp[:, 3], start=False, stop=True).then_inc(bank_full, 1)
                wait_bank_free(pe, us)
                for f in range(4):
                    pe.matmul(bank(us), Yc[:, 1 + f, cc], tab[:, f, 0, :], start=(f == 0), stop=False)
                    last = pe.matmul(bank(us), Yn[:, 1 + f, cc], tab[:, f, 1, :], start=False, stop=(f == 3))
                last.then_inc(bank_full, 1)
            pe.wait_ge(ld_lr, 16 * 4)
            for j, d in enumerate("fb"):
                both(f"lr{d}p", f"lr{d}s", RANK,
                     [(w_lr[:, k, j * RANK:(j + 1) * RANK], hT[:, k, 0:LP], hT[:, k, LP:T]) for k in range(KD)])
            wait_w(pe, ("in", W_QK))
            for c in range(4):
                both(f"qk{c}p", f"qk{c}s", P,
                     [(wtile(("in", W_QK))[:, k, c * P:(c + 1) * P], hT[:, k, 0:LP], hT[:, k, LP:T]) for k in range(KD)])
            pe.wait_ge(ld_gw, 16)
            for u in ("lrfp", "lrfs", "lrbp", "lrbs"):
                wait_drained(pe, u)
            for j in range(4):
                both(f"la{j}p", f"la{j}s", P, [(gw2[:, j * P:(j + 1) * P], lr_sb[:, j // 2, 0:LP], lr_sb[:, j // 2, LP:T])])
            modulations(4, NADA)
            pe.wait_ge(qe_ready, 1)
            for c in range(NT):
                transposes(f"kT{c}", [ek[:, j, rows(c)] for j in range(4)])
            for c in range(NT):
                wait_drained(pe, f"kT{c}")
            for t in range(NT):
                wait_drained(pe, f"v{t}")
            for c, d in KV_ORDER:
                u = f"kv{c}{d}"
                wait_bank_free(pe, u)
                for kt in range(2):
                    last = pe.matmul(bank(u, kt * 256, kt * 256 + 256), keT[:, c, "fb".index(d) * 2 + kt, :],
                                     v_sb[:, c, kt * 256:kt * 256 + 256], start=True, stop=True)
                last.then_inc(bank_full, 1)

            def chunk_out(c):
                u = f"o{c}"
                pe.wait_ge(am_ready, c + 1)
                if c == 0:
                    pe.wait_ge(sp_ready, 1)
                wait_bank_free(pe, u)
                for kt in range(2):
                    pair = bank(u, 256 * kt, 256 * kt + 256)
                    if c:
                        for j in range(2):
                            pe.matmul(pair, eq[:, 2 * j + kt, rows(c)], spd[:, j, c - 1, kt].rearrange("p x e -> p (x e)"),
                                      start=(j == 0), stop=False, skip_group_check=True)
                    for h in (2 * kt, 2 * kt + 1):
                        hc = slice(h * P, (h + 1) * P)
                        last = pe.matmul(bank(u, h * P, (h + 1) * P), am[:, c % 2, 0, hc], v_sb[:, c, hc],
                                         start=(c == 0), stop=True, skip_group_check=True)
                last.then_inc(bank_full, 1)

            for c in range(NT):
                for x in range(2):
                    u = f"at{c}{x}"
                    r = slice(64 * x, 64 * x + 64)
                    wait_bank_free(pe, u)
                    for q in range(4):
                        last = pe.matmul(bank(u, q * P, (q + 1) * P), ek[r, q, rows(c)], eq[r, q, rows(c)],
                                         start=True, stop=True)
                    last.then_inc(bank_full, 1)
                if c:
                    chunk_out(c - 1)
            chunk_out(NT - 1)

            n = 0
            for g in range(2):
                for s in range(2):
                    for h in range(2):
                        u = f"gr{g}{s}{h}"
                        pe.wait_ge(diag_ready, n + 1)
                        wait_bank_free(pe, u)
                        pe.matmul(bank(u), ones_m[:], diag[:, n % 2], start=True, stop=True).then_inc(bank_full, 1)
                        n += 1
            for c in range(NT):
                pe.wait_ge(o_ready, c + 1)
                transposes(f"ot{c}", [o_sb[:, c, h * P:(h + 1) * P] for h in range(HEADS)])
            pe.wait_ge(hy_done, 2 * CT)
            for c in range(NT):
                wait_drained(pe, f"ot{c}")
            for h in range(2):
                wait_w(pe, ("out", 512 * h))
            for kind, t in MIX_ORDER:
                if kind == "mix":
                    for h in range(2):
                        u = f"mx{h}{t}"
                        wait_bank_free(pe, u)
                        for k in range(KD):
                            last = pe.matmul(bank(u), mixT[:, k, rows(t)], wtile(("out", 512 * h))[:, k, :],
                                             start=(k == 0), stop=(k == KD - 1))
                        last.then_inc(bank_full, 1)
                else:
                    pe.wait_ge(xn2_ready, t + 1)
                    for h in range(2):
                        transposes(f"tr2_{t}{h}", [mix_sb[:, t, (4 * h + j) * P:(4 * h + j + 1) * P] for j in range(4)])
            pe.wait_ge(ld_keys, 16)

            def key_scores(h):
                wait_drained(pe, f"q{h}p")
                wait_drained(pe, f"q{h}s")
                wait_bank_free(pe, f"sc{h}p")
                pe.matmul(bank(f"sc{h}p", 0, NKEYS), qbuf[:, h % 2, 0:LP], keysT[:, h, :], start=True, stop=True
                          ).then_inc(bank_full, 1)
                wait_bank_free(pe, f"sc{h}s")
                for t in range(1, NT):
                    last = pe.matmul(bank(f"sc{h}s", (t - 1) * NKEYS, t * NKEYS), qbuf[:, h % 2, rows(t)],
                                     keysT[:, h, :], start=True, stop=True)
                last.then_inc(bank_full, 1)

            def three_parts(ua, ub, whi_, wlo_):
                wait_bank_free(pe, ua)
                wait_bank_free(pe, ub)
                for k in range(KD):
                    for j, (w, h) in enumerate(((whi_, h2hi), (whi_, h2lo), (wlo_, h2hi))):
                        st, en = k == 0 and j == 0, k == KD - 1 and j == 2
                        first = pe.matmul(bank(ua, 0, TH), w[:, k, :], h[:, k, 0:TH], start=st, stop=en)
                        last = pe.matmul(bank(ub, 0, TH), w[:, k, :], h[:, k, TH:T], start=st, stop=en)
                first.then_inc(bank_full, 1)
                last.then_inc(bank_full, 1)

            pe.wait_ge(h2lo_ready, NT)
            for h in range(HP):
                pe.wait_ge(qwhi_ready, h + 1)
                pe.wait_ge(qwlo_ready, h + 1)
                three_parts(f"q{h}p", f"q{h}s", qwhi[:, h % 2], qwlo[:, h % 2])
                if h:
                    key_scores(h - 1)
            key_scores(HP - 1)

            for b in range(8):
                pe.wait_ge(drained[b], len([u for u in order if unit[u] % 8 == b]))
            def first_products(n, b, first):
                pe.wait_ge(uhi_ready, n + 1)
                pe.wait_ge(ulo_ready, n + 1)
                if not (first and b < 2):
                    pe.wait_ge(gelu_done, n - 1)
                hb = 2 * (b % 2)
                for k in range(KD):
                    parts = ((uhi, h2hi), (uhi, h2lo), (ulo, h2hi))
                    for j, (w, h) in enumerate(parts):
                        st, en = k == 0 and j == 0, k == KD - 1 and j == 2
                        for a in range(2):
                            last = pe.matmul(ps[:, hb + a, 0:TH], w[:, b % 2, k, :], h[:, k, a * TH:(a + 1) * TH], start=st, stop=en)
                last.then_inc(h_full, 1)

            def step_a(it, first):
                for b in range(NB_BODY_A):
                    first_products(it * NB_BODY_A + b, b, first)

            loop(pe, IT_A, step_a)

            for t in range(NT):
                pe.wait_ge(sel_ready, t + 1)
                if t:
                    pe.wait_ge(cl_drained, t)
                for j in range(3):
                    last = pe.transpose(ps[:, 6, j * P:(j + 1) * P], selw[:, t, j, :], ident[:])
                last.then_inc(cl_full, 1)

            def step_b(it, first):
                for b in range(NB_BODY_B):
                    first_products(it * NB_BODY_B + b + BLK_A, b, False)
                    for q in range(TOK_BLK):
                        tok = it * NB_BODY_B * TOK_BLK + b * TOK_BLK + q
                        quad = b * 2 + q // 4
                        if q % 4 == 0 and not (first and quad < 2):
                            pe.wait_ge(gate_staged, it * 32 + quad - 1)
                        pe.wait_ge(onehot_ready, tok + 1)
                        o_ = ps[:, 4 + quad % 2, (q % 4) * P:(q % 4 + 1) * P]
                        for j in range(3):
                            last = pe.matmul(o_, eB[:, q], eA[:, j, q], start=(j == 0), stop=(j == 2))
                        last.then_inc(onehot_used, 1)

            loop(pe, IT_B, step_b)

            pe.wait_ge(gelu_done, NBLK)
            pe.wait_ge(gate_staged, T // 4)

            def step_2(it, first):
                for g in range(2):
                    pe.wait_ge(whi_ready, it * 2 * GRP + (g + 1) * GRP)
                    pe.wait_ge(wlo_ready, it * 2 * GRP + (g + 1) * GRP)
                    pe.wait_ge(vhi_ready, it * 2 * GRP + (g + 1) * GRP)
                    pe.wait_ge(vlo_ready, it * 2 * GRP + (g + 1) * GRP)
                    for u in range(2 * NT):
                        t, h = u // 2, u % 2
                        uu = g * 2 * NT + u
                        if not (first and uu < 5):
                            pe.wait_ge(y_added, it * 4 * NT + uu - 4)
                        for b in range(GRP):
                            for j, (w, v) in enumerate(((whi, vhi), (whi, vlo), (wlo, vhi))):
                                last = pe.matmul(ps[:, uu % 5, :], w[:, g, b, rows(t)], v[:, g, b, h * 512:(h + 1) * 512],
                                                 start=(b == 0 and j == 0), stop=(b == GRP - 1 and j == 2))
                        last.then_inc(y_full, 1)

            loop(pe, IT_2, step_2)

        PI = 3.1415925
        MAGIC = 12582912.0

        @block.vector
        def _(dve):
            chain = [0]

            def seq(ins):
                chain[0] += 1
                ins.then_inc(seq_dve, 1)
                dve.wait_ge(seq_dve, chain[0])

            def rsqrt_mean(row, n, width, ms, rt, parts=1):
                v = stat[:, row, 0:n]
                if parts == 2:
                    seq(dve.tensor_tensor(v, v, stat[:, row, n:2 * n], ALU.add))
                dve.tensor_scalar(v, v, 1.0 / width, EPS, ALU.mult, ALU.add).then_inc(ms, 1)
                dve.wait_ge(rt, 1)
                seq(dve.reciprocal(v, v))

            dve.memset(ones_m[:], 1.0).then_inc(const_ready, 1)
            dve.wait_ge(ld_filt, 16 * 5)
            for layer, (name, b) in enumerate((("fa", 0), ("fb", 1))):
                for s in "ps":
                    c0, c1 = seq_cols(s)
                    u = f"{name}_{s}"
                    wait_unit(dve, u)
                    dve.tensor_scalar(ft[:, 0, c0:c1], bank(u, 0, c1 - c0)[0:HID], hfc[:, b:b + 1], hfc[:, 2:3],
                                      ALU.add, ALU.mult).then_inc(drain_of(u), 1)
                for s in "ps":
                    wait_drained(dve, f"{name}_{s}")
                seq(dve.tensor_scalar(ft[:, 1], ft[:, 0], 1 / (2 * math.pi), MAGIC, ALU.mult, ALU.add))
                seq(dve.tensor_scalar(ft[:, 1], ft[:, 1], MAGIC, -2 * math.pi, ALU.subtract, ALU.mult))
                seq(dve.tensor_tensor(ft[:, 0], ft[:, 0], ft[:, 1], ALU.add))
                dve.tensor_scalar(ft[:, 0], ft[:, 0], PI, -PI, ALU.min, ALU.max).then_inc(f_arg, 1)
                dve.wait_ge(f_sin, layer + 1)
            dve.wait_ge(ld_dec, 16)
            for t in range(NT):
                for j, d in enumerate("fb"):
                    u = f"fc{t}{d}"
                    wait_unit(dve, u)
                    dve.tensor_tensor(ytmp[:, j], bank(u), dec_sb[:, t], ALU.mult).then_inc(drain_of(u), 1)
                wait_drained(dve, f"fc{t}b")
                if t < 2:
                    seq(dve.memset(ytmp[0:1, 1], 0.0))
                dve.tensor_tensor(kp[:, t], ytmp[:, 0], ytmp[:, 1], ALU.add)
                dve.tensor_tensor(km[:, t], ytmp[:, 0], ytmp[:, 1], ALU.subtract).then_inc(kpm_ready, 1)
                dve.wait_ge(kpm_ready, t + 1)
            dve.wait_ge(ssq1, NT)
            rsqrt_mean(0, NT, D, ms1, rt1)
            for t in range(NT):
                dve.tensor_scalar(x_sb[:, t], x_sb[:, t], stat[:, 0, t:t + 1], None, ALU.mult).then_inc(xn_ready, 1)

            def modulation(i):
                u = f"adc{i}"
                wait_unit(dve, u)
                seq_pair = bank(u, 0, 8).rearrange("p (c s) -> p c s", s=2)
                dve.tensor_tensor(mod[:, 4 * i:4 * i + 4, :], seq_pair,
                                  colv[:, C_BADA + 4 * i:C_BADA + 4 * i + 4].unsqueeze(2).broadcast_to([P, 4, 2]),
                                  ALU.add).then_inc(drain_of(u), 1)
                wait_drained(dve, u)

            dve.wait_ge(ld_small, 16 * 3)
            for i in range(4):
                modulation(i)

            def modulated(dst, c, g):
                seq(dve.scalar_tensor_tensor(dst[:], mod[:, c:c + KD, :], 1.0,
                                             colv[:, g:g + KD].unsqueeze(2).broadcast_to([P, KD, 2]), ALU.add, ALU.mult))

            modulated(scale1, KD, C_PRE1)
            for h in range(2):
                u = f"tr1_p{h}"
                wait_unit(dve, u)
                for j in range(4):
                    k = 4 * h + j
                    last = dve.tensor_scalar(hT[:, k, 0:LP], bank(u, j * P, (j + 1) * P), scale1[:, k, 0:1],
                                             mod[:, k, 0:1], ALU.mult, ALU.add)
                last.then_inc(drain_of(u), 1)
            for k in range(KD):
                u = f"tr1_{k}"
                wait_unit(dve, u)
                dve.tensor_scalar(hT[:, k, LP:T], bank(u), scale1[:, k, 1:2], mod[:, k, 1:2],
                                  ALU.mult, ALU.add).then_inc(drain_of(u), 1)

            n = 0
            for c in range(3 * CT):
                dst = (x0, x1, z)[c // CT]
                for s in "ps":
                    u = f"hy{c}{s}"
                    c0, c1 = seq_cols(s)
                    w = LP if s == "p" else ROW
                    d_ = dst[:, c % CT, c0:c1].rearrange("p (r w) -> p r w", w=w)
                    p_ = bank(u, 0, c1 - c0).rearrange("p (r w) -> p r w", w=w)
                    n += 1
                    dve.wait_ge(hyc1, n)
                    cw = C_CW + c
                    seq(dve.scalar_tensor_tensor(d_[:, :, 1:w], p_[:, :, 0:w - 1], colv[:, cw:cw + 1],
                                                 d_[:, :, 1:w], ALU.mult, ALU.add))
                    cw = C_CW + 2 * 3 * CT + c
                    dve.scalar_tensor_tensor(d_[:, :, 0:w - 1], p_[:, :, 1:w], colv[:, cw:cw + 1],
                                             d_[:, :, 0:w - 1], ALU.mult, ALU.add).then_inc(drain_of(u), 1)
            for s in "ps":
                wait_drained(dve, f"hy{3 * CT - 1}{s}")
            for c in range(CT):
                dve.tensor_tensor(z[:, c], z[:, c], x1[:, c], ALU.mult).then_inc(z_ready, 1)

            for f in range(NT):
                uc, us = f"zd{f}c", f"zd{f}s"
                wait_drained(dve, f"kd{f}c")
                wait_drained(dve, f"kd{f}s")
                wait_unit(dve, uc)
                seq(dve.tensor_tensor(ytmp[:, 0], bank(uc), Kcs[:, f, 0], ALU.mult))
                wait_unit(dve, us)
                seq(dve.tensor_tensor(ytmp[:, 1], bank(us), Kcs[:, f, 1], ALU.mult))
                seq(dve.tensor_tensor(Yc[:, f], ytmp[:, 0], ytmp[:, 1], ALU.subtract))
                dve.tensor_tensor(ytmp[:, 0], bank(uc), Kcs[:, f, 1], ALU.mult).then_inc(drain_of(uc), 1)
                dve.tensor_tensor(ytmp[:, 1], bank(us), Kcs[:, f, 0], ALU.mult).then_inc(drain_of(us), 1)
                wait_drained(dve, uc)
                wait_drained(dve, us)
                dve.tensor_tensor(Yn[:, f], ytmp[:, 0], ytmp[:, 1], ALU.add).then_inc(y_ready, 1)
                dve.wait_ge(y_ready, f + 1)
            n = 0
            for c in range(CT):
                for s in "ps":
                    u = f"yi{c}{s}"
                    c0, c1 = seq_cols(s)
                    wait_unit(dve, u)
                    dve.scalar_tensor_tensor(ytmp[:, n % 2, 0:c1 - c0], z[:, c, c0:c1], colv[:, C_HB + c:C_HB + c + 1],
                                             bank(u, 0, c1 - c0), ALU.mult, ALU.add).then_inc(drain_of(u), 1)
                    wait_drained(dve, u)
                    dve.tensor_tensor(mixT[:, c, c0:c1], ytmp[:, n % 2, 0:c1 - c0], x0[:, c, c0:c1],
                                      ALU.mult).then_inc(hy_done, 1)
                    n += 1
                    dve.wait_ge(hy_done, n)

            for j in range(4):
                for s in "ps":
                    u = f"la{j}{s}"
                    c0, c1 = seq_cols(s)
                    wait_unit(dve, u)
                    b = colv[:, C_GB + j:C_GB + j + 1]
                    dve.tensor_scalar(eq[:, j, c0:c1], bank(u, 0, c1 - c0), b, None, ALU.add)
                    dve.tensor_scalar(la[:, j, c0:c1], bank(u, 0, c1 - c0), b, 0.0, ALU.add, ALU.min
                                      ).then_inc(drain_of(u), 1)
            for s in "ps":
                wait_drained(dve, f"la3{s}")
            dve.scalar_tensor_tensor(eq[:], la[:], -2.0, eq[:], ALU.mult, ALU.add).then_inc(ax_ready, 1)
            dve.wait_ge(ln_done, 1)
            seq(dve.tensor_tensor(la[:], la[:], eq[:], ALU.subtract))
            for i in range(4, 5):
                modulation(i)
            ones_b = ones_m[:, 0:P]
            for j in range(4):
                for c in range(NT):
                    src, dst = la[:, j, c * P:(c + 1) * P], bc[:, j, c * P:(c + 1) * P]
                    if j >= 2:
                        src, dst = src[:, ::-1], dst[:, ::-1]
                    last = dve.tensor_tensor_scan(dst, ones_b, src, 0.0, ALU.mult, ALU.add)
            seq(last)
            bc4 = bc[:, :, :].rearrange("p j (c t) -> p j c t", t=P)
            seq(dve.tensor_scalar(hbend[:, 0:2], bc4[:, 0:2, :, P - 1], 0.5, None, ALU.mult))
            dve.tensor_scalar(hbend[:, 2:4], bc4[:, 2:4, :, 0], 0.5, None, ALU.mult).then_inc(hb_ready, 1)
            dve.wait_ge(hb_ready, 1)
            for j in range(4):
                last = dve.tensor_tensor(bc4[:, j], bc4[:, j], hbend[:, j].unsqueeze(2).broadcast_to([P, NT, P]), ALU.subtract)
            last.then_inc(bc_ready, 1)
            modulation(5)
            dve.wait_ge(exp_done, 1)
            for c in range(4):
                for s in "ps":
                    wait_drained(dve, f"qk{c}{s}")
            for j in range(2):
                dve.tensor_tensor(ek[:, 2 * j:2 * j + 2], ek[:, 2 * j:2 * j + 2], qk[:, 2:4], ALU.mult)
            for j in range(2):
                last = dve.tensor_tensor(eq[:, 2 * j:2 * j + 2], eq[:, 2 * j:2 * j + 2], qk[:, 0:2], ALU.mult)
            last.then_inc(qe_ready, 1)
            for i in range(6, NADA):
                modulation(i)
            dve.wait_ge(ld_state, 16)

            def er_of(r, j, c):
                return er[r, 2 * j:2 * j + 2, c].unsqueeze(2).broadcast_to([r.stop - r.start, 2, P])

            dve.wait_ge(spd_zero, 1)

            def before_chunk(j, c):
                for h in range(2):
                    r = slice(64 * h, 64 * h + 64)
                    last = dve.tensor_tensor(spd[r, j, c - 1, :, h], s_cur[r, j], er_of(r, j, c), ALU.mult)
                return last

            for c, d in KV_ORDER:
                u = f"kv{c}{d}"
                j = "fb".index(d)
                if c:
                    seq(before_chunk(j, c))
                wait_unit(dve, u)
                for h in range(2):
                    r = slice(64 * h, 64 * h + 64)
                    kv = bank(u)[r].rearrange("p (k x e) -> p k x e", k=2, x=2)[:, :, h, :]
                    if c:
                        last = dve.tensor_tensor(s_cur[r, j], kv, spd[r, j, c - 1, :, h], ALU.add)
                    else:
                        last = dve.tensor_tensor(st_out[r, j], kv, er_of(r, j, 0), ALU.mult)
                last.then_inc(drain_of(u), 1)
                wait_drained(dve, u)
                if c:
                    seq(dve.tensor_tensor(s_cur[:, j], s_cur[:, j], er_of(slice(0, P), j, c), ALU.mult))
                else:
                    dve.sem_inc(st_out_ready, 1)
            before_chunk(0, NT - 1)
            before_chunk(1, 1).then_inc(sp_ready, 1)

            for c in range(NT):
                if c >= 2:
                    wait_unit(dve, f"o{c - 2}")
                for x in range(2):
                    u = f"at{c}{x}"
                    wait_unit(dve, u)
                    for j in range(2):
                        last = dve.tensor_tensor(am[:, c % 2, j].rearrange("p (k x t) -> p k x t", x=2, t=P)[:, :, x],
                                                 bank(u, 256 * j, 256 * j + 256).rearrange("p (k t) -> p k t", t=P),
                                                 mask[:, j].unsqueeze(1).broadcast_to([P, 2, P]), ALU.mult)
                    last.then_inc(drain_of(u), 1)
                wait_drained(dve, f"at{c}0")
                wait_drained(dve, f"at{c}1")
                dve.tensor_tensor(am[:, c % 2, 0], am[:, c % 2, 0], am[:, c % 2, 1], ALU.add).then_inc(am_ready, 1)
                dve.wait_ge(am_ready, c + 1)
            for c in range(NT):
                wait_drained(dve, f"o{c}")
                seq(dve.tensor_tensor(osq[:, c], o_sb[:, c], o_sb[:, c], ALU.mult))
                seq(dve.tensor_reduce(stat[:, 1, 4 * c:4 * c + 4], osq[:, c].rearrange("p (h e) -> p h e", e=DV), AX_X, ALU.add))
            rsqrt_mean(1, NT * HEADS, DV, o_ms, o_rt)
            dve.wait_ge(gate_ready, NT)
            for c in range(NT):
                seq(dve.tensor_tensor(o_sb[:, c].rearrange("p (h e) -> p h e", e=DV), o_sb[:, c].rearrange("p (h e) -> p h e", e=DV),
                                      stat[:, 1, 4 * c:4 * c + 4].unsqueeze(2).broadcast_to([P, HEADS, DV]), ALU.mult))
                dve.tensor_tensor(o_sb[:, c], o_sb[:, c], og_sb[:, c], ALU.mult).then_inc(o_ready, 1)
            modulated(scale2, 4 * KD, C_PRE2)
            for g, (c, w) in enumerate(((2 * KD, C_POST1), (5 * KD, C_POST2))):
                seq(dve.tensor_tensor(gcol[:, g], mod[:, c:c + KD, :],
                                      colv[:, w:w + KD].unsqueeze(2).broadcast_to([P, KD, 2]), ALU.mult))
            n = 0
            names = [f"gr{g}{s}{h}" for g in range(2) for s in range(2) for h in range(2)]
            for g in range(2):
                for s in range(2):
                    for h in range(2):
                        if n >= 2:
                            wait_unit(dve, names[n - 2])
                        dve.tensor_tensor(diag[:, n % 2].rearrange("p (k n) -> p k n", n=P),
                                          ident[:].unsqueeze(1).broadcast_to([P, 4, P]),
                                          gcol[:, g, 4 * h:4 * h + 4, s].unsqueeze(2).broadcast_to([P, 4, P]),
                                          ALU.mult).then_inc(diag_ready, 1)
                        n += 1
            dve.wait_ge(ld_xr, 16)
            for u in names:
                wait_drained(dve, u)

            def rsqrt_of(v, ms, rt, n):
                dve.tensor_scalar(v, v, 1.0 / D, EPS, ALU.mult, ALU.add).then_inc(ms, 1)
                dve.wait_ge(rt, n)
                seq(dve.reciprocal(v, v))

            def mixed(t):
                dve.wait_ge(mix_ssq, t + 1)
                v = stat[:, 2, t:t + 1]
                seq(dve.tensor_tensor(v, stat[:, 2, 8 + 2 * t:9 + 2 * t], stat[:, 2, 9 + 2 * t:10 + 2 * t], ALU.add))
                rsqrt_of(v, mix_ms, mix_rt, t + 1)
                seq(dve.scalar_tensor_tensor(mix_sb[:, t], mix_sb[:, t], v, g1row[:, seq_of(t)], ALU.mult, ALU.mult))
                dve.tensor_tensor(x_sb[:, t], x_sb[:, t], mix_sb[:, t], ALU.add).then_inc(x1_ready, 1)
                dve.wait_ge(x1_ssq, t + 1)
                v = stat[:, 3, t:t + 1]
                rsqrt_of(v, x1_ms, x1_rt, t + 1)
                dve.tensor_scalar(mix_sb[:, t], x_sb[:, t], v, None, ALU.mult).then_inc(xn2_ready, 1)

            def turned(t):
                s = seq_of(t)
                for h in range(2):
                    u = f"tr2_{t}{h}"
                    wait_unit(dve, u)
                    for j in range(4):
                        k = 4 * h + j
                        last = dve.tensor_scalar(h2T[:, k, t * P:(t + 1) * P], bank(u, j * P, (j + 1) * P), scale2[:, k, s:s + 1],
                                                 mod[:, 3 * KD + k, s:s + 1], ALU.mult, ALU.add)
                    last.then_inc(drain_of(u), 1)

            for kind, t in MIX_ORDER:
                (mixed if kind == "mix" else turned)(t)
            for h in range(HP):
                up, us = f"sc{h}p", f"sc{h}s"
                wait_unit(dve, up)
                dve.tensor_copy(scores[:, 0, h], bank(up, 0, NKEYS)).then_inc(drain_of(up), 1)
                wait_unit(dve, us)
                dve.tensor_copy(scores[:, 1:NT, h], bank(us).rearrange("p (t n) -> p t n", n=NKEYS)).then_inc(drain_of(us), 1)
            wait_drained(dve, f"sc{HP - 1}p")
            wait_drained(dve, f"sc{HP - 1}s")

            dve.wait_ge(h2lo_ready, NT)
            val4 = sval[:].rearrange("p (h w) k -> p h w k", w=2)
            best = work[:, 0]
            pos = work[:, 1].bitcast(U32)
            for t in range(NT):
                for h in range(HP):
                    s_ = scores[:, t, h]
                    seq(dve.max(sval[:, h, 0:8], s_))
                    seq(dve.match_replace(srep[:], sval[:, h, 0:8], s_, NEG))
                    dve.max_index(sidx[:, h, 0:8], sval[:, h, 0:8], s_)
                    seq(dve.max(sval[:, h, 8:16], srep[:]))
                    seq(dve.max_index(sidx[:, h, 8:16], sval[:, h, 8:16], srep[:]))
                seq(dve.tensor_copy(itopf[:], sidx[:]))
                seq(dve.tensor_tensor(cand[:], val4[:, :, 0, :].unsqueeze(3).broadcast_to([P, PH, 16, 16]),
                                      val4[:, :, 1, :].unsqueeze(2).broadcast_to([P, PH, 16, 16]), ALU.add))
                for h in range(PH):
                    c_ = cand[:, h].rearrange("p a b -> p (a b)")
                    b0, b1 = best[:, 16 * h:16 * h + 8], best[:, 16 * h + 8:16 * h + 16]
                    seq(dve.max(b0, c_))
                    seq(dve.match_replace(crep[:], b0, c_, NEG))
                    dve.max_index(pos[:, 16 * h:16 * h + 8], b0, c_)
                    seq(dve.max(b1, crep[:]))
                    seq(dve.max_index(pos[:, 16 * h + 8:16 * h + 16], b1, crep[:]))
                bv = best.rearrange("p (h k) -> p h k", k=TOPK)
                seq(dve.tensor_tensor(selw[:, t, 2].rearrange("p (h k) -> p h k", k=TOPK), bv,
                                      bv[:, :, 0:1].broadcast_to([P, PH, TOPK]), ALU.subtract))
                i4 = itopf[:].rearrange("p (h w) k -> p h w k", w=2)
                for j in range(2):
                    dst = work[:, 2 + j].bitcast(U32)
                    if j == 0:
                        seq(dve.tensor_scalar(dst, pos, 4, None, ALU.logical_shift_right))
                    else:
                        seq(dve.tensor_scalar(dst, pos, 15, None, ALU.bitwise_and))
                    seq(dve.tensor_copy(work[:, 5], dst))
                    seq(dve.tensor_tensor(oneh[:], work[:, 5].unsqueeze(2).broadcast_to([P, HK, 16]),
                                          iota[:, 0:16].unsqueeze(1).broadcast_to([P, HK, 16]), ALU.is_equal))
                    o4 = oneh[:].rearrange("p (h k) a -> p h k a", k=TOPK)
                    seq(dve.tensor_tensor(o4, o4, i4[:, :, j, :].unsqueeze(2).broadcast_to([P, PH, TOPK, 16]), ALU.mult))
                    seq(dve.tensor_reduce(selw[:, t, j], oneh[:], AX_X, ALU.add))
            dve.sem_inc(topk_exp_in, 1)
            dve.wait_ge(topk_exp, 1)
            for t in range(NT):
                ev = selw[:, t, 2].rearrange("p (h k) -> p h k", k=TOPK)
                seq(dve.tensor_reduce(work[:, 2, 0:PH], ev, AX_X, ALU.add))
                seq(dve.reciprocal(work[:, 2, 0:PH], work[:, 2, 0:PH]))
                dve.tensor_tensor(ev, ev, work[:, 2, 0:PH].unsqueeze(2).broadcast_to([P, PH, TOPK]), ALU.mult
                                  ).then_inc(sel_ready, 1)
                dve.wait_ge(sel_ready, t + 1)
            for t in range(NT):
                dve.wait_ge(cl_full, t + 1)
                c3 = cols_hk[:, 0:3, t * P:(t + 1) * P]
                dve.tensor_copy(c3, ps[:, 6, 0:3 * P].rearrange("p (j n) -> p j n", j=3)).then_inc(cl_drained, 1)
                dve.wait_ge(cl_drained, t + 1)
                g_ = cols_hk[:, 2, t * P:(t + 1) * P]
                seq(dve.tensor_copy(part[:, 0], g_))
                seq(dve.tensor_tensor(rest[:], g_, part[:, 0], ALU.subtract))
                dve.tensor_copy(g_, part[:, 0])
                seq(dve.tensor_copy(part[:, 1], rest[:]))
                dve.tensor_tensor(g3col[:, t * P:(t + 1) * P], rest[:], part[:, 1], ALU.subtract)
                seq(dve.tensor_copy(cols_hk[:, 3, t * P:(t + 1) * P], part[:, 1]))
            seq(dve.tensor_copy(iota_b[:], iota[:]))

            def step_b(it, first):
                for q in range(NB_BODY_B * TOK_BLK):
                    tok = it * NB_BODY_B * TOK_BLK + q
                    if not (first and q < RING):
                        dve.wait_ge(onehot_used, tok + 1 - RING)
                    s = q % RING
                    col = bass.ds(tok, 1)
                    dve.tensor_scalar(eB[:, s], iota_b[:], cols_hk[:, 1, col], None, ALU.is_equal)
                    for j, g in enumerate((cols_hk[:, 2, col], cols_hk[:, 3, col], g3col[:, col])):
                        last = dve.tensor_scalar(eA[:, j, s], iota_b[:], cols_hk[:, 0, col], g, ALU.is_equal, ALU.mult)
                    last.then_inc(onehot_ready, 1)

            loop(dve, IT_B, step_b)

            dve.wait_ge(onehot_used, T)
            dve.wait_ge(h_full, NBLK)
            dve.memset(yacc[:], 0.0).then_inc(yacc_clear, 1)
            dve.wait_ge(yacc_clear, 1)

            def split_weights(it, b, first):
                n = it * 2 * GRP + b
                s = b % 4
                dve.wait_ge(a_landed[s], it * 32 + 16 * (b // 4 + 1))
                dve.wait_ge(g_landed[s], it * 32 + 16 * (b // 4 + 1))
                dve.tensor_tensor(ain[:, s], ain[:, s], gin[:, s], ALU.mult).then_inc(w_ready, 1)
                dve.wait_ge(whi_ready, n + 1)
                dve.tensor_tensor(wlo[:, b // GRP, b % GRP], ain[:, s], whi[:, b // GRP, b % GRP].bitcast(F32),
                                  ALU.subtract).then_inc(wlo_ready, 1)

            def add_up(it, g, last=False):
                for u in range(2 * NT):
                    t, h = u // 2, u % 2
                    uu = g * 2 * NT + u
                    dve.wait_ge(y_full, it * 4 * NT + uu + 1)
                    y_ = yacc[:, t, h * 512:(h + 1) * 512]
                    dve.tensor_tensor(y_, ps[:, uu % 5, :], y_, ALU.add).then_inc(y_added, 1)
                    if last and h == 1 and t:
                        finish(t - 1)
                if last:
                    finish(NT - 1)

            def finish(t):
                dve.wait_ge(y_ssq, t + 1)
                v = stat[:, 0, t:t + 1]
                rsqrt_of(v, y_ms, y_rt, t + 1)
                seq(dve.scalar_tensor_tensor(yacc[:, t], yacc[:, t], v, g2row[:, seq_of(t)], ALU.mult, ALU.mult))
                dve.tensor_tensor(yacc[:, t], yacc[:, t], x_sb[:, t], ALU.add).then_inc(y_fin, 1)

            for b in range(GRP):
                split_weights(0, b, True)

            def step_2(it, first, last):
                for b in range(GRP, 2 * GRP):
                    split_weights(it, b, first)
                add_up(it, 0)
                if not last:
                    for b in range(GRP):
                        split_weights(it + 1, b, False)
                add_up(it, 1, last)

            step_2(0, True, False)
            with dve.Fori(1, IT_2 - 1) as it:
                step_2(it, False, False)
            step_2(IT_2 - 1, False, True)

        @block.scalar
        def _(act):
            chain = [0]

            def seq(ins):
                chain[0] += 1
                ins.then_inc(seq_act, 1)
                act.wait_ge(seq_act, chain[0])

            def move(u, dst, src=None, func=ACT.Copy, **kw):
                wait_unit(act, u)
                act.activation(dst, bank(u) if src is None else src, func, **kw).then_inc(drain_of(u), 1)

            def mod_row(i):
                if i >= 2:
                    wait_unit(act, f"adc{i - 2}")
                move(f"ada{i}", modrow[:, i % 2], bank(f"ada{i}")[0:2])
                wait_drained(act, f"ada{i}")
                act.sem_inc(modrow_ready, 1)

            act.wait_ge(ld_small, 16 * 3)
            act.activation(cs[:], cin[:], ACT.Silu).then_inc(cs_ready, 1)
            for layer in range(2):
                act.wait_ge(f_arg, layer + 1)
                act.activation(fh[:, layer], ft[:, 0], ACT.Sin).then_inc(f_sin, 1)
            act.wait_ge(ld_x, 16)
            for t in range(NT):
                if t:
                    act.wait_ge(ssq1, t)
                act.activation(Kscr[:], x_sb[:, t], ACT.Square,
                               accum_out=stat[:, 0, t:t + 1]).then_inc(ssq1, 1)
            act.wait_ge(ms1, 1)
            act.activation(stat[:, 0, 0:NT], stat[:, 0, 0:NT], ACT.Sqrt).then_inc(rt1, 1)

            for i in range(4):
                mod_row(i)
            for c in range(3 * CT):
                dst = (x0, x1, z)[c // CT]
                for s in "ps":
                    u = f"hy{c}{s}"
                    c0, c1 = seq_cols(s)
                    wait_unit(act, u)
                    act.activation(dst[:, c % CT, c0:c1], bank(u, 0, c1 - c0), ACT.Identity,
                                   bias=colv[:, C_CB + c:C_CB + c + 1],
                                   scale=colv[:, C_CW + 3 * CT + c:C_CW + 3 * CT + c + 1]).then_inc(hyc1, 1)

            for f in range(NT):
                for j, d in enumerate("cs"):
                    move(f"kd{f}{d}", Kcs[:, f, j])
            for t in range(NT):
                move(f"v{t}", v_sb[:, t])
            for t in range(NT):
                move(f"zt{t}", zt[:, t])
            for t in range(NT):
                move(f"og{t}", og_sb[:, t], func=ACT.Silu)
            act.wait_ge(y_ready, NT)
            for j, d in enumerate("fb"):
                for s in "ps":
                    c0, c1 = seq_cols(s)
                    u = f"lr{d}{s}"
                    move(u, lr_sb[:, j, c0:c1], bank(u, 0, c1 - c0)[0:RANK])
            act.wait_ge(hy_done, 2 * CT)
            for c in range(4):
                for s in "ps":
                    c0, c1 = seq_cols(s)
                    u = f"qk{c}{s}"
                    move(u, qk[:, c, c0:c1], bank(u, 0, c1 - c0), scale=DK ** -0.5 if c < 2 else 1.0)
            act.wait_ge(ax_ready, 1)
            seq(act.activation(eq[:], eq[:], ACT.Exp, scale=-1.0))
            act.activation(eq[:], eq[:], ACT.Ln, bias=1.0).then_inc(ln_done, 1)
            for i in range(4, 7):
                mod_row(i)
            act.wait_ge(hb_ready, 1)
            act.activation(er[:], hbend[:], ACT.Exp, scale=1 / GATE_NORM).then_inc(er_ready, 1)
            act.wait_ge(bc_ready, 1)
            act.activation(ek[:], bc[:], ACT.Exp, scale=-1 / GATE_NORM)
            act.activation(eq[:], bc[:], ACT.Exp, scale=1 / GATE_NORM).then_inc(exp_done, 1)
            for i in range(7, NADA):
                mod_row(i)
            for c in range(NT):
                move(f"kT{c}", keT[:, c].rearrange("p j n -> p (j n)"))
            for c in range(NT):
                move(f"o{c}", o_sb[:, c])
            act.wait_ge(o_ms, 1)
            act.activation(stat[:, 1, 0:NT * HEADS], stat[:, 1, 0:NT * HEADS], ACT.Sqrt).then_inc(o_rt, 1)
            for g, row in enumerate((g1row, g2row)):
                for s in range(2):
                    for h in range(2):
                        move(f"gr{g}{s}{h}", row[:, s, h * 512:(h + 1) * 512])
            for c in range(NT):
                move(f"ot{c}", mixT[:, CT:KD, c * P:(c + 1) * P], bank(f"ot{c}").rearrange("p (h t) -> p h t", t=P))

            def mixed(t):
                for h in range(2):
                    u = f"mx{h}{t}"
                    wait_unit(act, u)
                    seq(act.activation(sq_scr[:, 0:512], bank(u), ACT.Square, accum_out=stat[:, 2, 8 + 2 * t + h:9 + 2 * t + h]))
                    act.activation(mix_sb[:, t, h * 512:(h + 1) * 512], bank(u), ACT.Copy).then_inc(drain_of(u), 1)
                    wait_drained(act, u)
                act.sem_inc(mix_ssq, 1)
                act.wait_ge(mix_ms, t + 1)
                act.activation(stat[:, 2, t:t + 1], stat[:, 2, t:t + 1], ACT.Sqrt).then_inc(mix_rt, 1)
                act.wait_ge(x1_ready, t + 1)
                act.activation(sq_scr[:], x_sb[:, t], ACT.Square, accum_out=stat[:, 3, t:t + 1]).then_inc(x1_ssq, 1)
                act.wait_ge(x1_ms, t + 1)
                act.activation(stat[:, 3, t:t + 1], stat[:, 3, t:t + 1], ACT.Sqrt).then_inc(x1_rt, 1)

            def turned(t):
                for h in range(2):
                    wait_drained(act, f"tr2_{t}{h}")
                act.activation(h2hi[:, :, t * P:(t + 1) * P], h2T[:, :, t * P:(t + 1) * P], ACT.Copy).then_inc(h2hi_ready, 1)

            for kind, t in MIX_ORDER:
                if kind == "mix":
                    mixed(t)
            for t in range(NT):
                turned(t)

            def split_q(h):
                l = ("q", 512 * (h // 4))
                if h % 4 == 0:
                    wait_w(act, l)
                if h >= 2:
                    wait_unit(act, f"q{h - 2}s")
                act.activation(qwhi[:, h % 2], wtile(l)[:, :, (h % 4) * P:(h % 4 + 1) * P], ACT.Copy).then_inc(qwhi_ready, 1)

            act.wait_ge(h2lo_ready, NT)
            split_q(0)
            for h in range(HP):
                if h + 1 < HP:
                    split_q(h + 1)
                if h >= 2:
                    wait_unit(act, f"sc{h - 2}s")
                for a, s in enumerate("ps"):
                    u = f"q{h}{s}"
                    move(u, qbuf[:, h % 2, a * TH:(a + 1) * TH], bank(u, 0, TH))

            def split_u(n, b, first):
                act.wait_ge(u_landed[b % 4], n_round(n, b))
                if not (first and b < 2):
                    act.wait_ge(h_full, n - 1)
                    act.wait_ge(ulo_ready, n - 1)
                act.activation(uhi[:, b % 2], uraw[:, b % 4], ACT.Copy).then_inc(uhi_ready, 1)

            def n_round(n, b):
                return (n - b % 4) * 4 + 16

            def gelu(n, b, first):
                act.wait_ge(h_full, n + 1)
                if not first:
                    act.wait_ge(a_stored[b % 4], (n - b % 4) * 4)
                hb = 2 * (b % 2)
                act.activation(aout[:, b % 4].rearrange("p (a t) -> p a t", a=2), ps[:, hb:hb + 2, 0:TH],
                               ACT.Gelu_apprx_tanh).then_inc(gelu_done, 1)

            split_u(0, 0, True)

            def pair(n, b, first, first_split):
                split_u(n + 1, b + 1, first_split)
                gelu(n, b, first)

            def stage(it, b, first):
                for q in range(2):
                    quad = 2 * b + q
                    act.wait_ge(onehot_used, it * 128 + 4 * (quad + 1))
                    half, off = b // 8, (quad % 16) * 4
                    if quad % 16 == 0 and not first:
                        act.wait_ge(g_stored[half], it * 16)
                    act.activation(gst[:, half, :, off:off + 4], ps[:, 4 + quad % 2, :].rearrange("p (q i) -> p i q", q=4),
                                   ACT.Copy).then_inc(gate_staged, 1)

            for b in range(NB_BODY_A):
                pair(b, b, True, b == 0)
            with act.Fori(1, IT_A) as it:
                for b in range(NB_BODY_A):
                    pair(it * NB_BODY_A + b, b, False, False)
            act.wait_ge(topk_exp_in, 1)
            act.activation(selw[:, :, 2], selw[:, :, 2], ACT.Exp).then_inc(topk_exp, 1)

            def step_b(it, first, last):
                for b in range(NB_BODY_B):
                    n = it * NB_BODY_B + b + BLK_A
                    if last and b == NB_BODY_B - 1:
                        gelu(n, b, False)
                    else:
                        pair(n, b, False, False)
                    stage(it, b, first)

            step_b(0, True, False)
            with act.Fori(1, IT_B - 1) as it:
                step_b(it, False, False)
            step_b(IT_B - 1, False, True)

            act.wait_ge(yacc_clear, 1)

            def high_parts(it, b, first):
                n = it * 2 * GRP + b
                g, s = b // GRP, b % 4
                if not first:
                    act.wait_ge(y_full, it * 4 * NT - 2 * NT * (2 - g) + 2 * NT)
                act.wait_ge(v_landed[s], it * 32 + 16 * (b // 4 + 1))
                act.activation(vhi[:, g, b % GRP], vraw[:, s], ACT.Copy).then_inc(vhi_ready, 1)
                act.wait_ge(w_ready, n + 1)
                act.activation(whi[:, g, b % GRP], ain[:, s], ACT.Copy).then_inc(whi_ready, 1)

            def step_2(it, first):
                for b in range(2 * GRP):
                    high_parts(it, b, first)

            loop(act, IT_2, step_2)
            act.wait_ge(vlo_ready, NBLK)
            for t in range(NT):
                act.wait_ge(y_added, IT_2 * 4 * NT - 2 * NT + 2 * (t + 1))
                act.activation(vraw[:, t % 2], yacc[:, t], ACT.Square, accum_out=stat[:, 0, t:t + 1]).then_inc(y_ssq, 1)
                act.wait_ge(y_ms, t + 1)
                act.activation(stat[:, 0, t:t + 1], stat[:, 0, t:t + 1], ACT.Sqrt).then_inc(y_rt, 1)

        @block.gpsimd
        def _(pool):
            pool.wait_ge(ld_lr, 16 * 4)
            for t in range(NT):
                wait_drained(pool, f"og{t}")
                o_ = og_sb[:, t].rearrange("p (h e) -> p h e", e=DV)
                pool.tensor_tensor(o_, o_, gnrow[:].unsqueeze(1).broadcast_to([P, HEADS, DV]), ALU.mult).then_inc(gate_ready, 1)
            wait_unit(pool, f"yi{CT - 1}s")
            pool.memset(spd[:], 0.0).then_inc(spd_zero, 1)
            for t in range(NT):
                tt = slice(t * P, (t + 1) * P)
                pool.wait_ge(h2hi_ready, t + 1)
                pool.tensor_tensor(h2lo[:, :, tt], h2T[:, :, tt], h2hi[:, :, tt].bitcast(F32), ALU.subtract).then_inc(h2lo_ready, 1)

            for h in range(HP):
                l = ("q", 512 * (h // 4))
                pool.wait_ge(qwhi_ready, h + 1)
                if h % 4 == 0:
                    wait_w(pool, l)
                pool.tensor_tensor(qwlo[:, h % 2], wtile(l)[:, :, (h % 4) * P:(h % 4 + 1) * P], qwhi[:, h % 2].bitcast(F32),
                                   ALU.subtract).then_inc(qwlo_ready, 1)

            def split_u(n, b, first):
                pool.wait_ge(uhi_ready, n + 1)
                if not (first and b < 2):
                    pool.wait_ge(h_full, n - 1)
                pool.tensor_tensor(ulo[:, b % 2], uraw[:, b % 4], uhi[:, b % 2].bitcast(F32), ALU.subtract).then_inc(ulo_ready, 1)

            def step_u(it, first):
                for b in range(4):
                    split_u(it * 4 + b, b, first)

            loop(pool, NBLK // 4, step_u)

            pool.wait_ge(yacc_clear, 1)

            def step_2(it, first):
                for b in range(2 * GRP):
                    n = it * 2 * GRP + b
                    g = b // GRP
                    pool.wait_ge(vhi_ready, n + 1)
                    pool.tensor_tensor(vlo[:, g, b % GRP], vraw[:, b % 4], vhi[:, g, b % GRP].bitcast(F32), ALU.subtract
                                       ).then_inc(vlo_ready, 1)

            loop(pool, IT_2, step_2)


def shape_constants():
    f32 = np.float32
    dec, feat = [], []
    deltas = np.abs(np.linspace(math.log(1e-2) / 1.5, math.log(1e-2) / 0.3, HY, dtype=f32))
    for L in (LP, LS):
        t = np.linspace(0.0, 1.0, L, dtype=f32)[:, None]
        dec.append(np.exp(-t * deltas[None, :]).astype(f32))
        bands = (EMB - 1) // 2
        w = (f32(2.0 * math.pi) * np.arange(L, dtype=f32)[:, None] / f32(L)).astype(f32)
        f = np.linspace(1e-4, bands - 1, bands, dtype=f32)[None, :]
        a = (f * w).astype(f32)
        feat.append(np.concatenate([t, np.cos(a), -np.sin(a)], axis=-1).astype(f32).T)
    decay = np.concatenate(dec).reshape(NT, P, HY).transpose(1, 0, 2)

    def tables(L):
        ang = np.pi * np.outer(np.arange(L), 2 * np.arange(L) + 1) / (2 * L)
        return np.cos(ang), np.sin(ang)

    C, S = tables(LS)
    fwd = np.stack([C, S], 1).reshape(4, P, 2, LS).transpose(1, 0, 2, 3)
    inv = np.stack([C.T / LS, S.T / LS], 1).reshape(4, P, 2, LS).transpose(1, 0, 2, 3)
    C, S = tables(LP)
    tabp = np.stack([C, S, C.T / LP, S.T / LP], 1)
    s = np.arange(P)
    masks = np.stack([s[:, None] <= s[None, :], s[:, None] >= s[None, :]], 1)
    c = {"zfeat": np.concatenate(feat, 1), "decay": decay, "tab_fwd": fwd, "tab_inv": inv, "tab_p": tabp,
         "masks": masks, "ident": np.eye(P), "iota": np.broadcast_to(np.arange(P), (P, P))}
    return {k: np.ascontiguousarray(v, dtype=f32) for k, v in c.items()}


def kernel(**inputs):
    import concourse.bacc as _bacc
    from concourse.bass_utils import run_bass_kernel_spmd as _run

    a = {k: np.asarray(v) for k, v in inputs.items()}

    def columns(v):
        return v.reshape(-1, P).T

    cols = [columns(a["b_ada"][0]), columns(a["norm_pre1"][0]), columns(a["norm_pre2"][0]),
            columns(a["norm_post1"][0]), columns(a["norm_post2"][0]),
            columns(a["hy_conv_w"][0].reshape(-1)), columns(a["hy_conv_b"][0]), columns(a["hy_bias"][0]),
            columns(a["gla_b_f"][0]), columns(a["gla_b_b"][0])]
    data = {
        "x": np.concatenate([a["x_prompt"][0], a["x_sample"][0]]),
        "cvec": np.stack([columns(a["c_ctx"]), columns(a["c"][0])], 2),
        "w_ada": a["w_ada"][0], "w_in": a["w_in"][0], "w_out": a["w_out"][0], "w_q": a["peer_wq"][0],
        "cols": np.concatenate(cols, 1),
        "hfcols": np.stack([a["hf_b1"][0], a["hf_b2"][0], a["hf_freq"][0]], 1),
        "hf_w1": a["hf_w1"][0], "hf_w2": a["hf_w2"][0], "hf_w3": a["hf_w3"][0],
        "gla_w2": np.concatenate([a["gla_w2_f"][0], a["gla_w2_b"][0]], 1),
        "gnorm": a["gla_norm"][0],
        "state": a["state_gla"][0, 0].reshape(2, 2, 2, DK, DV).transpose(2, 3, 0, 1, 4).reshape(P, 2, 2, DV),
        "keys_t": a["peer_keys"][0].reshape(HP, NKEYS, 128).transpose(2, 0, 1),
        "u_t": a["peer_u"][0].reshape(NBLK, 128, KD, P).transpose(0, 3, 2, 1),
        "v_tab": a["peer_v"][0],
    }
    data.update(shape_constants())
    nc = _bacc.Bacc("TRN2", target_bir_lowering=False, num_devices=1)
    arrays, args = {}, []
    for name, v in data.items():
        arrays[f"in_{name}"] = np.ascontiguousarray(v)
        args.append(nc.dram_tensor(f"in_{name}", v.shape, F32, kind="ExternalInput").ap())
    outs = [("out_x", [T, D]), ("out_state", [1, 1, 2, HEADS, DK, DV])]
    for name, shape in outs:
        args.append(nc.dram_tensor(name, shape, F32, kind="ExternalOutput").ap())
    build(nc, args)
    r = _run(nc, [arrays], core_ids=[0])
    y = r.results[0]["out_x"]
    return y[None, :LP], y[None, LP:], r.results[0]["out_state"]


def build(nc, args):
    args[-1] = args[-1].rearrange("b l q h d e -> (b l) q h d e")
    bass_hybrid_layer(nc, *args)
```
